# Optimizing a Trainium2 kernel written in Bass

```python
import jax, jax.numpy as jnp
from jax import lax
import numpy as np

D_MODEL = 2048
BATCH = 1
SEQ = 256
DEPTH = 1

CHUNK = 64
MEM_LEN = 256
EPS = 1e-6
LRU_WIDTH = 1024
LRU_BLOCKS = 16
LRU_BLOCK = LRU_WIDTH // LRU_BLOCKS
CONV_WIDTH = 4
LRU_C = 8.0
ATTN_HEADS = 16
ATTN_KV_HEADS = 4
HEAD_DIM = 64
GQA_GROUP = ATTN_HEADS // ATTN_KV_HEADS
ATTN_WIDTH = ATTN_HEADS * HEAD_DIM
KV_WIDTH = ATTN_KV_HEADS * HEAD_DIM
WINDOW = 128
WINDOW_CHUNKS = WINDOW // CHUNK
MIX_WIDTH = LRU_WIDTH + ATTN_WIDTH
IN_WIDTH = 2 * LRU_WIDTH + ATTN_WIDTH + 2 * KV_WIDTH
MEM_HEADS = 4
MEM_HEAD_DIM = D_MODEL // MEM_HEADS
D_FF = -(-8 * D_MODEL // (3 * 256)) * 256
NEG_INF = -1e30

kernel_name = "hymba_rglru_swa_sink_alibi_memxattn_swiglu"

def rmsnorm(x, g):
    x32 = x.astype(jnp.float32)
    var = jnp.mean(x32 * x32, axis=-1, keepdims=True)
    return (x32 * lax.rsqrt(var + EPS) * g.astype(jnp.float32)).astype(x.dtype)

def _lin_combine(c1, c2):
    a1, b1 = c1
    a2, b2 = c2
    return a1 * a2, a2 * b1 + b2

def rglru_group(xb, gate, conv_w, conv_b, w_rgate, b_rgate, w_igate, b_igate, lru_lambda):
    B, S, _ = xb.shape
    xpad = jnp.pad(xb, ((0, 0), (CONV_WIDTH - 1, 0), (0, 0)))
    xc = conv_b + sum(xpad[:, j:j + S] * conv_w[j] for j in range(CONV_WIDTH))
    xr = xc.reshape(B, S, LRU_BLOCKS, LRU_BLOCK)
    r = jax.nn.sigmoid(jnp.einsum('bshi,hij->bshj', xr, w_rgate).reshape(B, S, LRU_WIDTH) + b_rgate)
    i = jax.nn.sigmoid(jnp.einsum('bshi,hij->bshj', xr, w_igate).reshape(B, S, LRU_WIDTH) + b_igate)
    log_a = -LRU_C * r.astype(jnp.float32) * jax.nn.softplus(-lru_lambda.astype(jnp.float32))
    a = jnp.exp(log_a)
    mult = jnp.sqrt(-jnp.expm1(2.0 * log_a))
    bterm = mult * (i * xc).astype(jnp.float32)
    _, h = lax.associative_scan(_lin_combine, (a, bterm), axis=1)
    return h.astype(xb.dtype) * jax.nn.gelu(gate)

def swa_sink_group(q, k, v, sinks):
    B, S, _ = q.shape
    NC = S // CHUNK
    qc = q.reshape(B, NC, CHUNK, ATTN_KV_HEADS, GQA_GROUP, HEAD_DIM)
    kc = k.reshape(B, NC, CHUNK, ATTN_KV_HEADS, HEAD_DIM)
    vc = v.reshape(B, NC, CHUNK, ATTN_KV_HEADS, HEAD_DIM)

    def band(t):
        parts = [jnp.pad(t, ((0, 0), (j, 0), (0, 0), (0, 0), (0, 0)))[:, :NC]
                 for j in reversed(range(WINDOW_CHUNKS))]
        return jnp.concatenate(parts, axis=2)

    kb, vb = band(kc), band(vc)
    scores = jnp.einsum('bnqkgd,bnskd->bnkgqs', qc, kb).astype(jnp.float32) * (HEAD_DIM ** -0.5)
    slopes = 2.0 ** (-8.0 * jnp.arange(1, ATTN_HEADS + 1, dtype=jnp.float32) / ATTN_HEADS)
    slopes = slopes.reshape(ATTN_KV_HEADS, GQA_GROUP)[:, :, None, None]
    dist = jnp.abs(jnp.arange(CHUNK)[:, None] + (WINDOW_CHUNKS - 1) * CHUNK
                   - jnp.arange(WINDOW)[None, :]).astype(jnp.float32)
    scores = scores - slopes * dist
    key_chunk = jnp.arange(NC)[:, None] - (WINDOW_CHUNKS - 1) + jnp.arange(WINDOW)[None, :] // CHUNK
    valid = (key_chunk >= 0)[None, :, None, None, None, :]
    scores = jnp.where(valid, scores, NEG_INF)
    sink = jnp.broadcast_to(sinks.astype(jnp.float32).reshape(ATTN_KV_HEADS, GQA_GROUP)[:, :, None, None],
                            scores.shape[:-1] + (1,))
    p = jax.nn.softmax(jnp.concatenate([scores, sink], axis=-1), axis=-1)[..., :WINDOW]
    out = jnp.einsum('bnkgqs,bnskd->bnqkgd', p.astype(v.dtype), vb)
    return out.reshape(B, S, ATTN_WIDTH)

def memory_cross_attention(xn, memn, w_mq, w_mkv, w_mo):
    B, S, _ = xn.shape
    q = (xn @ w_mq).reshape(B, S, MEM_HEADS, MEM_HEAD_DIM)
    kv = memn @ w_mkv
    k = kv[..., :D_MODEL].reshape(B, MEM_LEN, MEM_HEADS, MEM_HEAD_DIM)
    v = kv[..., D_MODEL:].reshape(B, MEM_LEN, MEM_HEADS, MEM_HEAD_DIM)
    s = jnp.einsum('bshd,bmhd->bhsm', q, k).astype(jnp.float32) * (MEM_HEAD_DIM ** -0.5)
    p = jax.nn.softmax(s, axis=-1).astype(v.dtype)
    o = jnp.einsum('bhsm,bmhd->bshd', p, v).reshape(B, S, D_MODEL)
    return o @ w_mo

def swiglu(xn, w_gate_up, w_down):
    gu = xn @ w_gate_up
    return (jax.nn.silu(gu[..., :D_FF]) * gu[..., D_FF:]) @ w_down

def setup_inputs(seed: int = 0) -> dict:
    key = jax.random.key(seed)
    ks = jax.random.split(key, 24)
    L = DEPTH

    def nrm(k, shape, scale):
        return jax.random.normal(k, shape, jnp.float32) * scale

    u = jax.random.uniform(ks[11], (L, LRU_WIDTH), jnp.float32, minval=0.9, maxval=0.999)
    a0 = u ** (1.0 / LRU_C)
    lru_lambda = jnp.log(a0) - jnp.log1p(-a0)
    return {
        "x": nrm(ks[0], (BATCH, SEQ, D_MODEL), 1.0),
        "mem": nrm(ks[1], (BATCH, MEM_LEN, D_MODEL), 1.0),
        "norm_mix": 1.0 + nrm(ks[2], (L, D_MODEL), 0.05),
        "w_in": nrm(ks[3], (L, D_MODEL, IN_WIDTH), D_MODEL ** -0.5),
        "conv_w": nrm(ks[4], (L, CONV_WIDTH, LRU_WIDTH), CONV_WIDTH ** -0.5),
        "conv_b": nrm(ks[5], (L, LRU_WIDTH), 0.01),
        "w_rgate": nrm(ks[6], (L, LRU_BLOCKS, LRU_BLOCK, LRU_BLOCK), LRU_BLOCK ** -0.5),
        "b_rgate": nrm(ks[7], (L, LRU_WIDTH), 0.01),
        "w_igate": nrm(ks[8], (L, LRU_BLOCKS, LRU_BLOCK, LRU_BLOCK), LRU_BLOCK ** -0.5),
        "b_igate": nrm(ks[9], (L, LRU_WIDTH), 0.01),
        "lru_lambda": lru_lambda,
        "attn_sinks": nrm(ks[10], (L, ATTN_HEADS), 0.5),
        "w_out": nrm(ks[12], (L, MIX_WIDTH, D_MODEL), MIX_WIDTH ** -0.5),
        "norm_mem_q": 1.0 + nrm(ks[13], (L, D_MODEL), 0.05),
        "norm_mem_kv": 1.0 + nrm(ks[14], (L, D_MODEL), 0.05),
        "w_mq": nrm(ks[15], (L, D_MODEL, D_MODEL), D_MODEL ** -0.5),
        "w_mkv": nrm(ks[16], (L, D_MODEL, 2 * D_MODEL), D_MODEL ** -0.5),
        "w_mo": nrm(ks[17], (L, D_MODEL, D_MODEL), D_MODEL ** -0.5),
        "norm_ffn": 1.0 + nrm(ks[18], (L, D_MODEL), 0.05),
        "w_gate_up": nrm(ks[19], (L, D_MODEL, 2 * D_FF), D_MODEL ** -0.5),
        "w_down": nrm(ks[20], (L, D_FF, D_MODEL), D_FF ** -0.5),
        "norm_final": 1.0 + nrm(ks[21], (D_MODEL,), 0.05),
    }

def reference(x, mem, norm_mix, w_in, conv_w, conv_b, w_rgate, b_rgate, w_igate, b_igate,
              lru_lambda, attn_sinks, w_out, norm_mem_q, norm_mem_kv, w_mq, w_mkv, w_mo,
              norm_ffn, w_gate_up, w_down, norm_final):
    h = x
    o_gate = LRU_WIDTH
    o_q = 2 * LRU_WIDTH
    o_k = o_q + ATTN_WIDTH
    o_v = o_k + KV_WIDTH
    for l in range(DEPTH):
        n = rmsnorm(h, norm_mix[l])
        proj = n @ w_in[l]
        y_lru = rglru_group(proj[..., :o_gate], proj[..., o_gate:o_q], conv_w[l], conv_b[l],
                            w_rgate[l], b_rgate[l], w_igate[l], b_igate[l], lru_lambda[l])
        y_att = swa_sink_group(proj[..., o_q:o_k], proj[..., o_k:o_v], proj[..., o_v:], attn_sinks[l])
        h = h + jnp.concatenate([y_lru, y_att], axis=-1) @ w_out[l]
        h = h + memory_cross_attention(rmsnorm(h, norm_mem_q[l]), rmsnorm(mem, norm_mem_kv[l]),
                                       w_mq[l], w_mkv[l], w_mo[l])
        h = h + swiglu(rmsnorm(h, norm_ffn[l]), w_gate_up[l], w_down[l])
    return rmsnorm(h, norm_final)


_drawn_inputs = setup_inputs


def setup_inputs(seed=0):
    import zlib

    import numpy as np

    out = dict(_drawn_inputs(seed))
    spreads = {}
    factors = {'conv_b': 2.843,
     'b_rgate': 8.0,
     'b_igate': 8.0,
     'attn_sinks': 5.074,
     'norm_mem_q': 8.0,
     'norm_mem_kv': 7.091,
     'norm_ffn': 8.0}
    for name, (base, spread) in spreads.items():
        noise = np.random.default_rng([zlib.crc32(name.encode()), seed]).standard_normal(out[name].shape)
        drawn = base * np.exp(spread * noise) if base else spread * noise
        out[name] = __import__('jax').numpy.asarray(drawn.astype(out[name].dtype))
    for name, factor in factors.items():
        out[name] = (out[name] * factor).astype(out[name].dtype)
    return out
```

```python
from contextlib import ExitStack

import concourse.bass as bass
from concourse import mybir

F32 = mybir.dt.float32
F32R = mybir.dt.float32r
ALU = mybir.AluOpType
ACT = mybir.ActivationFunctionType
AX = mybir.AxisListType

P = 128
D = 2048
T = 256
KT = D // P
LRU = 1024
LT = LRU // P
CONV = 4
HEADS, KV_HEADS, HD = 16, 4, 64
CHUNK = 64
GROUP = HEADS // KV_HEADS
MH = 4
MHT = D // MH // P
D_FF = 5632
FT = D_FF // P
EPS = 1e-6
NEG = -1e30
UNIT = 2048
STAGES = 4
RING = 4
KB = 8

U_MK = 0
U_XB = U_MK + KT
U_MV = U_XB + LT
U_K = U_MV + 16
U_V = U_K + 2
U_Q = U_V + 2
U_GT = U_Q + 8
U_OUT = U_GT + LT
U_MQ = U_OUT + KT
U_MO = U_MQ + KT
U_GU = U_MO + KT
U_DN = U_GU + 2 * FT
DN_PARTS = [(0, 16), (16, 16), (32, 12)]

A_XB, A_MV = 0, LT
A_K = A_MV + 8
A_V, A_Q = A_K + 2, A_K + 4
A_GT = A_Q + 8
V_MK, V_OUT, V_MQ, V_MO, V_GU = 0, KT, 2 * KT, 3 * KT, 4 * KT
V_DN = V_GU + 2 * FT

DVE_OUT = [(0, 2), (2, 4), (6, 4)]
POOL_OUT = [(10, 2), (12, 4)]

GK = 2 * KV_HEADS


def hybrid_block(nc, xT, memT, w_units, w_down, gains, lru_par, w_gates, sinks, out):
    with ExitStack() as ctx:
        def sb(name, shape, dt=F32):
            return ctx.enter_context(nc.sbuf_tensor(name, shape, dt))

        def sem(name):
            return ctx.enter_context(nc.semaphore(name))

        stage = sb("stage", [P, STAGES, UNIT])
        w_hi = sb("w_hi", [P, RING, UNIT // 2], F32R)
        w_lo = sb("w_lo", [P, RING, UNIT // 2], F32R)
        acts = sb("acts", [P, 2, KT, T], F32R)
        act_hi, act_lo = acts[:, 0, :, :], acts[:, 1, :, :]
        g_all = sb("g_all", [P, 5, KT])
        par = sb("par", [P, 8, LT])
        lam4 = sb("lam4", [P, 6, LT])
        sink_b = sb("sink_b", [P, HEADS])
        ones = sb("ones", [P, P])
        ident = sb("ident", [P, P])
        eps_t = sb("eps_t", [P, 1])
        rms_inv = sb("rms_inv", [P, T])
        rms = sb("rms", [P, T])
        rms_col = sb("rms_col", [P, 2, 2])
        sq_sum = sb("sq_sum", [P, T])
        sq_tmp = rms
        gate_s = sb("gate_s", [P, T])
        up_s = sb("up_s", [P, T])
        small = sb("small", [P, 8, GROUP])
        msmall = sb("msmall", [P, 4, 2])

        base = (int(nc.sbuf_base) + 63) // 64 * 64

        def at(name, offset, shape, dt=F32):
            return nc.alloc_sbuf_tensor_at(name, shape, dt, offset=base + offset)

        K1 = 1024
        mem_k = at("mem_k", 0, [P, KT, T])
        mem_v = at("mem_v", 16 * K1, [P, 2, D])
        x_raw = at("x_raw", 16 * K1, [P, KT, T])
        alts = at("alts", 32 * K1, [P, 2, KT, T], F32R)
        alt_hi, alt_lo = alts[:, 0, :, :], alts[:, 1, :, :]
        hids = at("hids", 0, [P, 2, FT, T], F32R)
        hid_hi, hid_lo = hids[:, 0, :, :], hids[:, 1, :, :]
        S = 64 * K1
        h = at("h", S + 24 * K1, [P, KT, T])
        mem_raw = at("mem_raw", S + 24 * K1, [P, KT, T])
        sq_piece = at("sq_piece", S, [P, 4, T])
        sq_acc = at("sq_acc", S + 4 * K1, [P, 4, T])
        x_inv = at("x_inv", S + 8 * K1, [P, T])
        xc = at("xc", S, [P, LT, T])
        theta = at("theta", S + 8 * K1, [P, LT, T])
        wg = at("wg", S + 16 * K1, [P, 2, LT, P])
        root = at("root", S + 24 * K1, [P, 4, T])
        xpad = at("xpad", S + 28 * K1, [P, 2, 264])
        r_t = at("r_t", S + 31 * K1, [P, T])
        i_t = at("i_t", S + 32 * K1, [P, 2, T])
        den = at("den", S + 34 * K1, [P, 2, T])
        a_t = at("a_t", S + 36 * K1, [P, 2, T])
        b_t = at("b_t", S + 38 * K1, [P, 2, T])
        kd = at("kd", S + 8 * K1, [P, KV_HEADS, T])
        vd = at("vd", S + 12 * K1, [P, 2, KV_HEADS, 2, HD])
        pt = at("pt", S + 16 * K1, [P, 2, 2 * T])
        negdist = at("negdist", S + 20 * K1, [P, 3 * CHUNK])
        lru_g = at("lru_g", S + 21 * K1, [P, 2, T])
        qs = at("qs", 32 * K1, [P, 8, T])
        pb = at("pb", S + 24 * K1, [P, 4, GROUP, T])
        mq = at("mq", S, [P, 2, MHT, T])
        mp = at("mp", S + 8 * K1, [P, 2, T])
        mpt = at("mpt", S + 10 * K1, [P, 2, T])
        bank = [ctx.enter_context(nc.psum_tensor(f"bank{i}", [P, 512], F32)) for i in range(6)]
        o_bank = ctx.enter_context(nc.psum_tensor("o_bank", [P, 1024], F32))
        bank.append(o_bank[:, 0:512])
        bank.append(o_bank[:, 512:1024])

        weights_loaded = [sem(f"weights_loaded{s}") for s in range(STAGES)]
        w_hi_ready = sem("w_hi_ready")
        w_lo_ready = sem("w_lo_ready")
        blocks_used = sem("blocks_used")
        act_evacs = sem("act_evacs")
        dve_evacs = sem("dve_evacs")
        halves_taken = sem("halves_taken")
        first_block_loaded = sem("first_block_loaded")
        mem_landed = [sem(f"mem_landed{i}") for i in range(4)]
        x_landed = sem("x_landed")
        par_landed = sem("par_landed")
        gains_landed = sem("gains_landed")
        wg_landed = sem("wg_landed")
        res_landed = sem("res_landed")
        consts_ready = sem("consts_ready")
        mask_ready = sem("mask_ready")
        pads_ready = sem("pads_ready")
        mem_hi_ready = sem("mem_hi_ready")
        mem_lo_ready = sem("mem_lo_ready")
        pool_steps = sem("pool_steps")
        sq_ready = sem("sq_ready")
        sums_ready = sem("sums_ready")
        rms_ready = sem("rms_ready")
        inv_ready = sem("inv_ready")
        dve_steps = sem("dve_steps")
        x_norm = sem("x_norm")
        act_hi_ready = sem("act_hi_ready")
        act_lo_ready = sem("act_lo_ready")
        squared = sem("squared")
        summed = sem("summed")
        sp_exp = sem("sp_exp")
        lam_ready = sem("lam_ready")
        conv_ready = sem("conv_ready")
        gates_ready = sem("gates_ready")
        sig_ready = sem("sig_ready")
        theta_ready = sem("theta_ready")
        root_ready = sem("root_ready")
        root_used = sem("root_used")
        den_ready = sem("den_ready")
        lru_steps = sem("lru_steps")
        gated_in = sem("gated_in")
        mult_ready = sem("mult_ready")
        states_ready = sem("states_ready")
        y_lru_f = sem("y_lru_f")
        y_lru_hi = sem("y_lru_hi")
        y_lru_lo = sem("y_lru_lo")
        scores_ready = sem("scores_ready")
        max_ready = sem("max_ready")
        scores_taken = sem("scores_taken")
        probs_exp = sem("probs_exp")
        total_inv = sem("total_inv")
        probs_ready = sem("probs_ready")
        turned = sem("turned")
        pt_ready = sem("pt_ready")
        heads_ready = sem("heads_ready")
        y_att_hi = sem("y_att_hi")
        y_att_lo = sem("y_att_lo")
        m_scores = sem("m_scores")
        m_max = sem("m_max")
        m_exp = sem("m_exp")
        m_probs = sem("m_probs")
        m_turned = sem("m_turned")
        m_pt = sem("m_pt")
        m_heads = sem("m_heads")
        o_lo_ready = sem("o_lo_ready")
        silu_ready = sem("silu_ready")
        hid_ready = sem("hid_ready")
        hid_hi_ready = sem("hid_hi_ready")
        hid_lo_ready = sem("hid_lo_ready")
        last_squared = sem("last_squared")
        gained = sem("gained")
        outs_dve = sem("outs_dve")
        outs_pool = sem("outs_pool")
        stored = sem("stored")

        def turns_before(k):
            return 3 * (k // 2) + k % 2

        def head_cols(b, rows, half):
            return b[rows, :].rearrange("p (j e q) -> p j e q", j=2, e=2)[:, :, half, :]

        block = ctx.enter_context(nc.Block())

        @block.sync
        def _(sp):
            def mem_piece(n):
                sp.dma_start(mem_raw[:, 4 * n:4 * n + 4, :],
                             memT[:, 4 * n:4 * n + 4, :]).then_inc(mem_landed[n], 16)

            sp.dma_start(stage[:, 0, 0:KB * P], w_units[0, :, 0:KB * P]).then_inc(first_block_loaded, 16)
            sp.dma_start(g_all[:, :, :], gains).then_inc(gains_landed, 16)
            mem_piece(0)
            mem_piece(1)
            sp.dma_start(stage[:, 0, KB * P:], w_units[0, :, KB * P:]).then_inc(weights_loaded[0], 16)
            sp.dma_start(stage[:, 1, :], w_units[1]).then_inc(weights_loaded[1], 16)
            mem_piece(2)
            mem_piece(3)
            for s in range(2, STAGES):
                sp.dma_start(stage[:, s, :], w_units[s]).then_inc(weights_loaded[s], 16)
            with sp.Fori(1, U_DN // STAGES) as i:
                for s in range(STAGES):
                    sp.wait_ge(w_lo_ready, i * 8 + (2 * s - 6))
                    sp.dma_start(stage[:, s, :], w_units[i * STAGES + s]).then_inc(weights_loaded[s], 16)
            with sp.Fori(0, KT // 4) as i:
                for n in range(12):
                    first, tiles = DN_PARTS[n % 3]
                    sp.wait_ge(w_lo_ready, i * 24 + (2 * (U_DN + n) - 6))
                    sp.dma_start(stage[:, n % STAGES, 0:tiles * P],
                                 w_down[i * 4 + n // 3, :, first * P:(first + tiles) * P]
                                 ).then_inc(weights_loaded[n % STAGES], 16)
            for n, (first, tiles) in enumerate(DVE_OUT):
                sp.wait_ge(outs_dve, n + 1)
                sp.dma_start(out[:, first:first + tiles, :], h[:, first:first + tiles, :]).then_inc(stored, 16)
                if n < len(POOL_OUT):
                    first, tiles = POOL_OUT[n]
                    sp.wait_ge(outs_pool, n + 1)
                    sp.dma_start(out[:, first:first + tiles, :], h[:, first:first + tiles, :]).then_inc(stored, 16)
            sp.wait_ge(stored, 16 * (len(DVE_OUT) + len(POOL_OUT)))

        @block.gpsimd
        def _(pool):
            g = nc.gpsimd
            steps = [0]

            def step(ins):
                steps[0] += 1
                ins.then_inc(pool_steps, 1)
                pool.wait_ge(pool_steps, steps[0])

            g.memset(ones[:], 1.0).then_inc(consts_ready, 1)
            g.memset(eps_t[:], EPS).then_inc(consts_ready, 1)
            g.dma_start(par[:, :, :], lru_par).then_inc(par_landed, 16)
            g.dma_start(sink_b[:, :], sinks.partition_broadcast(P)).then_inc(par_landed, 16)
            step(g.memset(ident[:], 0.0))
            g.affine_select(out=ident[:], in_=ident[:], compare_op=ALU.not_equal, fill=1.0, base=0,
                            pattern=[[-1, P]], channel_multiplier=1).then_inc(consts_ready, 1)

            def squares(raw, landed, count):
                for n in range(4):
                    if count:
                        pool.wait_ge(landed, count)
                    else:
                        pool.wait_ge(landed[n], 16)
                    if n == 3 and not count:
                        g.dma_start(x_raw[:, :, :], xT).then_inc(x_landed, 16)
                    dst = sq_acc if n == 0 else sq_piece
                    step(g.tensor_tensor(dst[:, :, :], raw[:, 4 * n:4 * n + 4, :],
                                         raw[:, 4 * n:4 * n + 4, :], ALU.mult))
                    if n:
                        step(g.tensor_tensor(sq_acc[:, :, :], sq_acc[:, :, :], sq_piece[:, :, :], ALU.add))
                step(g.tensor_tensor(sq_acc[:, 0:2, :], sq_acc[:, 0:2, :], sq_acc[:, 2:4, :], ALU.add))

            squares(mem_raw, mem_landed, 0)
            g.tensor_tensor(sq_sum[:], sq_acc[:, 0, :], sq_acc[:, 1, :], ALU.add).then_inc(sq_ready, 1)
            pool.wait_ge(sq_ready, 1)
            squares(x_raw, x_landed, 16)
            pool.wait_ge(sums_ready, 2)
            g.tensor_tensor(sq_sum[:], sq_acc[:, 0, :], sq_acc[:, 1, :], ALU.add).then_inc(sq_ready, 1)

            pool.wait_ge(sq_ready, 2)
            step(g.memset(wg[:, :, :, :], 0.0))
            for half in range(2):
                rows = slice(half * HD, half * HD + HD)
                for gate in range(2):
                    g.dma_start(wg[rows, gate, :, half * HD:half * HD + HD],
                                w_gates[gate, half]).then_inc(wg_landed, 16)
            pool.wait_ge(mem_lo_ready, KT)
            g.memset(xpad[:, :, :], 0.0).then_inc(pads_ready, 1)

            def gate_input(c):
                pool.wait_ge(sig_ready, 2 * c + 2)
                pool.wait_ge(gates_ready, c + 1)
                pool.wait_ge(conv_ready, c + 1)
                g.tensor_tensor(xc[:, c, :], xc[:, c, :], i_t[:, c % 2, :], ALU.mult).then_inc(gated_in, 1)

            def multiplier(c):
                pool.wait_ge(root_ready, c // 4 + 1)
                pool.wait_ge(den_ready, c + 1)
                g.tensor_tensor(root[:, c % 4, :], root[:, c % 4, :], den[:, c % 2, :],
                                ALU.mult).then_inc(mult_ready, 1)

            for c in range(LT):
                gate_input(c)
            for c in range(LT):
                multiplier(c)

            pool.wait_ge(gates_ready, LT)
            pool.wait_ge(states_ready, LT)
            g.memset(pb[:, 1, :, 0:CHUNK], 0.0).then_inc(mask_ready, 1)
            g.memset(pb[:, 3, :, 0:CHUNK], 0.0).then_inc(mask_ready, 1)
            step(g.iota(negdist[:], pattern=[[1, 3 * CHUNK]], base=-CHUNK, channel_multiplier=-1,
                        allow_small_or_imprecise_dtypes=True))
            step(g.tensor_scalar(pt[:, 0, 0:3 * CHUNK], negdist[:], 2.0, 0.0, ALU.mult, ALU.max))
            step(g.tensor_tensor(negdist[:], negdist[:], pt[:, 0, 0:3 * CHUNK], ALU.subtract))
            step(g.memset(negdist[0:CHUNK, 2 * CHUNK:3 * CHUNK], NEG))
            g.memset(negdist[CHUNK:P, 0:CHUNK], NEG).then_inc(mask_ready, 1)

            for k in range(GK):
                L, off = (2, 3)[k % 2] * CHUNK, (k % 2) * CHUNK
                p = pb[:, k % 4, :, off:off + L]
                pool.wait_ge(total_inv, k + 1)
                g.tensor_tensor(p, p, small[:, 2 + k % 2, :].unsqueeze(2).broadcast_to([P, GROUP, L]),
                                ALU.mult).then_inc(probs_ready, 1)

            pool.wait_ge(turned, GK + GK // 2)
            g.dma_start(h[:, :, :], xT).then_inc(res_landed, 16)

            def square_tiles(phase, evacs, tiles=KT):
                pool.wait_ge(sums_ready, 3 + phase)
                step(g.memset(sq_sum[:], 0.0))
                with pool.Fori(0, tiles) as m:
                    pool.wait_ge(dve_evacs, m + (evacs + 1))
                    g.tensor_tensor(sq_tmp[:], h[:, m, :], h[:, m, :], ALU.mult).then_inc(squared, 1)
                    pool.wait_ge(squared, m + (KT * phase + 1))
                    g.tensor_tensor(sq_sum[:], sq_sum[:], sq_tmp[:], ALU.add).then_inc(summed, 1)
                    pool.wait_ge(summed, m + (KT * phase + 1))

            square_tiles(0, V_OUT)
            square_tiles(1, V_MO)
            square_tiles(2, V_DN, KT - 1)
            pool.wait_ge(inv_ready, 6)
            pool.wait_ge(gained, KT)
            for first, tiles in POOL_OUT:
                o = h[:, first:first + tiles, :]
                g.tensor_tensor(o, o, rms_inv[:].unsqueeze(1).broadcast_to([P, tiles, T]),
                                ALU.mult).then_inc(outs_pool, 1)

        @block.scalar
        def _(act):
            a = nc.scalar

            def hi_block(b, slot, stage_slot, count, tiles=KB, half=None):
                half = slot % 2 if half is None else half
                first = isinstance(b, int) and b == 0
                act.wait_ge(first_block_loaded if first else weights_loaded[stage_slot], count)
                if not isinstance(b, int) or b >= RING:
                    act.wait_ge(blocks_used, b - (RING - 1))
                a.copy(w_hi[:, slot, 0:tiles * P],
                       stage[:, stage_slot, half * KB * P:(half * KB + tiles) * P]).then_inc(w_hi_ready, 1)

            def hi_unit(u, s=None, mid=None):
                if s is None:
                    s = u % STAGES
                    count = 16 * (u // STAGES + 1)
                else:
                    count = (u - s) * (16 // STAGES) + 16
                hi_block(u * 2, (2 * s) % RING, s, count)
                if mid is not None:
                    mid()
                hi_block(u * 2 + 1, (2 * s + 1) % RING, s, count)

            def take_rms(n):
                act.wait_ge(sums_ready, n)
                if n > 2:
                    act.wait_ge(inv_ready, n - 1)
                a.activation(rms[:], bank[7][:, 0:T], ACT.Sqrt, bias=eps_t[:, 0:1],
                             scale=1.0 / D).then_inc(rms_ready, 1)

            def mem_hi(pieces):
                for n in pieces:
                    act.wait_ge(mem_landed[n], 16)
                    for k in range(4 * n, 4 * n + 4):
                        a.activation(alt_hi[:, k, :], mem_raw[:, k, :], ACT.Copy,
                                     scale=g_all[:, 2, k:k + 1]).then_inc(mem_hi_ready, 1)

            act.wait_ge(consts_ready, 3)
            a.activation(rms_col[:, 0, 0:1], eps_t[:, 0:1], ACT.Sqrt)
            hi_block(0, 0, 0, 16)
            act.wait_ge(gains_landed, 16)
            mem_hi((0, 1))
            hi_block(1, 1, 0, 16)
            hi_unit(1, mid=lambda: mem_hi((2,)))
            mem_hi((3,))
            for u in range(2, KT):
                hi_unit(u)
                if u == 4:
                    act.wait_ge(sums_ready, 2)
                    a.activation(rms_col[:, 0, :], bank[7][:, T:T + 2], ACT.Sqrt, bias=eps_t[:, 0:1],
                                 scale=1.0 / D).then_inc(rms_ready, 1)
                    take_rms(2)
                if u == 6:
                    act.wait_ge(lam_ready, 1)
                    a.activation(lam4[:, 1, :], lam4[:, 0, :], ACT.Exp, scale=-1.0).then_inc(sp_exp, 1)
                if u == 9:
                    take_rms(3)
                if u >= 12:
                    for k in range(4 * (u - 12), 4 * (u - 12) + 4):
                        act.wait_ge(x_norm, k + 1)
                        a.copy(act_hi[:, k, :], x_raw[:, k, :]).then_inc(act_hi_ready, 1)

            def sigmoids(c):
                act.wait_ge(gates_ready, c + 1)
                if c >= 1:
                    act.wait_ge(theta_ready, c)
                b = bank[4 + c % 2]
                a.activation(r_t[:], b[:, 0:T], ACT.Sigmoid, bias=par[:, 5, c:c + 1]).then_inc(sig_ready, 1)
                if c >= 2:
                    act.wait_ge(gated_in, c - 1)
                a.activation(i_t[:, c % 2, :], b[:, T:2 * T], ACT.Sigmoid,
                             bias=par[:, 6, c:c + 1]).then_inc(sig_ready, 1)
                act.wait_ge(sig_ready, 2 * c + 1)
                act.wait_ge(lam_ready, 2)
                a.activation(theta[:, c, :], r_t[:], ACT.Tanh, scale=lam4[:, 0, c:c + 1]).then_inc(theta_ready, 1)

            def roots(n):
                act.wait_ge(theta_ready, 4 * n + 4)
                if n:
                    act.wait_ge(root_used, 4)
                a.activation(root[:, :, :], theta[:, 4 * n:4 * n + 4, :], ACT.Sqrt).then_inc(root_ready, 1)

            def pad_tile(c):
                act.wait_ge(blocks_used, 2 * (U_XB + c) + 2)
                act.wait_ge(pads_ready, 1)
                if c >= 2:
                    act.wait_ge(conv_ready, c - 1)
                a.copy(xpad[:, c % 2, CONV - 1:CONV - 1 + T], bank[c % 4][:, 0:T]).then_inc(act_evacs, 1)

            for c in range(LT):
                hi_unit(U_XB + c)
                if c >= 2:
                    pad_tile(c - 2)
                if c >= 4:
                    sigmoids(c - 4)
            for u in range(16):
                hi_unit(U_MV + u)
                if u < 2:
                    pad_tile(LT - 2 + u)
                if u < 4:
                    sigmoids(4 + u)
                if u in (3, 10):
                    roots(u // 8)
                if u % 4 == 1 and u >= 5:
                    n = (u - 5) // 4
                    act.wait_ge(blocks_used, 2 * (U_MV + 4 * n) + 8)
                    act.wait_ge(inv_ready, 2)
                    for tt in range(2):
                        a.activation(mem_v[:, tt, 512 * n:512 * n + 512], bank[2 * (n % 2) + tt][:, :],
                                     ACT.Copy, scale=rms_col[:, 1, tt:tt + 1]).then_inc(act_evacs, 1)
            def keys(m):
                act.wait_ge(blocks_used, 2 * (U_K + m) + 2)
                act.wait_ge(states_ready, LT)
                for g in range(2):
                    for half in range(2):
                        ins = a.copy(kd[HD * half:HD * half + HD, 2 * m + g, :],
                                     bank[m][HD * g:HD * g + HD, 0:T])
                ins.then_inc(act_evacs, 1)

            def values():
                act.wait_ge(blocks_used, 2 * (U_V + 1) + 2)
                for tt in range(2):
                    src = bank[2 + tt][:, 0:T].rearrange("p (g d) -> p g d", g=KV_HEADS)
                    a.copy(vd[:, tt, :, 0, :], src)
                    a.copy(vd[:, tt, :, 1, :], src).then_inc(act_evacs, 1)

            def queries(j):
                act.wait_ge(blocks_used, 2 * (U_Q + j) + 2)
                a.activation(qs[:, j, :], bank[j % 4][:, 0:T], ACT.Copy,
                             scale=HD ** -0.5).then_inc(act_evacs, 1)

            def probs(k):
                L, off = (2, 3)[k % 2] * CHUNK, (k % 2) * CHUNK
                act.wait_ge(max_ready, k + 1)
                if k >= 2:
                    act.wait_ge(probs_ready, k - 1)
                for n in range(GROUP):
                    p = pb[:, k % 4, n, off:off + L]
                    a.activation(p, p, ACT.Exp, bias=small[:, k % 2, n:n + 1],
                                 accum_out=small[:, 2 + k % 2, n:n + 1])
                a.activation(small[:, 4 + k % 2, :], small[:, 4 + k % 2, :], ACT.Exp).then_inc(probs_exp, 1)

            def turn_evac(k):
                act.wait_ge(turned, turns_before(k + 1))
                if k >= 1:
                    act.wait_ge(heads_ready, k)
                a.copy(pt[:, 0, :], bank[6][:, :]).then_inc(pt_ready, 1)
                if k % 2:
                    a.copy(pt[:, 1, :], bank[7][:, :]).then_inc(pt_ready, 1)

            def heads_hi(k):
                g, t = k // 2, k % 2
                act.wait_ge(heads_ready, k + 1)
                for half in range(2):
                    rows = slice(half * HD, half * HD + HD)
                    ins = a.copy(alt_hi[rows, LT + 2 * g:LT + 2 * g + 2, t * P:t * P + P],
                                 head_cols(bank[6], rows, half))
                ins.then_inc(y_att_hi, 1)

            def gate_tile(c):
                act.wait_ge(blocks_used, 2 * (U_GT + c) + 2)
                if c >= 2:
                    act.wait_ge(y_lru_f, c - 1)
                a.activation(lru_g[:, c % 2, :], bank[c % 4][:, 0:T], ACT.Gelu_apprx_tanh).then_inc(act_evacs, 1)

            def y_hi(c):
                act.wait_ge(y_lru_f, c + 1)
                a.copy(alt_hi[:, c, :], xc[:, c, :]).then_inc(y_lru_hi, 1)

            def mid(j):
                if 0 <= j - 9 < GK:
                    heads_hi(j - 9)
                if j >= 12 and j % 2 == 0:
                    gate_tile(j - 12)
                    gate_tile(j - 11)
                    act.wait_ge(scores_ready, GK)
                    y_hi(j - 12)
                    y_hi(j - 11)

            for u in range(4):
                hi_unit(U_K + u)
                if u == 1:
                    act.wait_ge(blocks_used, 2 * (U_MV + 12) + 8)
                    for tt in range(2):
                        a.activation(mem_v[:, tt, 1536:2048], bank[2 + tt][:, :], ACT.Copy,
                                     scale=rms_col[:, 1, tt:tt + 1]).then_inc(act_evacs, 1)
                if u >= 2:
                    keys(u - 2)
            for j in range(16):
                hi_unit(U_Q + j, mid=lambda: mid(j))
                if j == 1:
                    values()
                if 2 <= j < 10:
                    queries(j - 2)
                if 0 <= j - 8 < GK:
                    turn_evac(j - 8)
                if 0 <= j - 5 < GK:
                    probs(j - 5)
            def h_hi(phase, m, plane):
                act.wait_ge(dve_evacs, m + ((V_OUT, V_MO)[phase] + 1))
                a.activation(act_hi[:, m, :], h[:, m, :], ACT.Copy,
                             scale=g_all[:, plane, bass.ds(m, 1)]).then_inc(act_hi_ready, 1)

            def h_loop(base_unit, phase, plane):
                with act.Fori(1, KT // 4) as i:
                    for s in range(4):
                        hi_unit(i * 4 + (base_unit + s), s)
                        h_hi(phase, i * 4 + (s - 2), plane)

            hi_unit(U_OUT, mid=lambda: mid(16))
            gate_tile(6)
            y_hi(6)

            def last_gate():
                gate_tile(7)
                y_hi(7)

            hi_unit(U_OUT + 1, mid=last_gate)
            for s in range(2, 4):
                hi_unit(U_OUT + s)
                h_hi(0, s - 2, 1)
            h_loop(U_OUT, 0, 1)

            def m_softmax(hd):
                act.wait_ge(m_max, hd + 1)
                if hd >= 1:
                    act.wait_ge(m_turned, hd)
                for tt in range(2):
                    a.activation(mp[:, tt, :], bank[4][:, tt * T:tt * T + T], ACT.Exp,
                                 bias=msmall[:, 1, tt:tt + 1], scale=(D // MH) ** -0.5,
                                 accum_out=msmall[:, 2, tt:tt + 1]).then_inc(m_exp, 1)

            def m_turn_evac(hd):
                act.wait_ge(m_turned, hd + 1)
                if hd >= 1:
                    act.wait_ge(m_heads, 2 * hd)
                a.copy(mpt[:, :, :], bank[5][:, :].rearrange("p (a t) -> p a t", a=2)).then_inc(m_pt, 1)

            for j in range(16):
                hi_unit(U_MQ + j)
                if j in (8, 12):
                    m_turn_evac((j - 8) // 4)
                if j < 2:
                    h_hi(0, 14 + j, 1)
                if j == 2:
                    take_rms(4)
                if j in (6, 10, 14):
                    m_softmax((j - 6) // 4)
            hi_unit(U_MO)
            m_turn_evac(2)
            hi_unit(U_MO + 1)
            m_softmax(3)
            for s in range(2, 4):
                hi_unit(U_MO + s, mid=(lambda: m_turn_evac(3)) if s == 2 else None)
                h_hi(1, s - 2, 3)
            h_loop(U_MO, 1, 3)

            def silu(p):
                act.wait_ge(dve_evacs, p * 2 + (V_GU + 1))
                a.activation(gate_s[:], gate_s[:], ACT.Silu).then_inc(silu_ready, 1)

            def hid_hi_tile(p):
                act.wait_ge(hid_ready, p + 1)
                a.copy(hid_hi[:, p, :], up_s[:]).then_inc(hid_hi_ready, 1)

            hi_unit(U_GU)
            h_hi(1, 14, 3)
            hi_unit(U_GU + 1)
            h_hi(1, 15, 3)
            hi_unit(U_GU + 2)
            take_rms(5)
            silu(0)
            hi_unit(U_GU + 3)
            hid_hi_tile(0)
            with act.Fori(1, FT // 2) as i:
                for s in range(4):
                    hi_unit(i * 4 + (U_GU + s), s)
                    if s % 2 == 0:
                        silu(i * 2 + (s // 2 - 1))
                    else:
                        hid_hi_tile(i * 2 + (s // 2 - 1))
            def hi_down(i, n):
                u = i * 12 + (U_DN + n)
                for half in range(2):
                    tiles = 4 if n % 3 == 2 and half else KB
                    hi_block(u * 2 + half, (2 * n + half) % RING, n % STAGES,
                             i * 48 + 16 * ((U_DN + n) // STAGES + 1), tiles, half)

            def gain_tile(m):
                act.wait_ge(dve_evacs, m + (V_DN + 1))
                if isinstance(m, int) and m == KT - 1:
                    act.wait_ge(last_squared, 1)
                else:
                    act.wait_ge(squared, m + (2 * KT + 1))
                a.activation(h[:, m, :], h[:, m, :], ACT.Copy,
                             scale=g_all[:, 4, bass.ds(m, 1)]).then_inc(gained, 1)

            def down_body(i, first):
                for n in range(12):
                    hi_down(i, n)
                    if n == 0 and first:
                        silu(FT - 1)
                    if n == 1 and first:
                        hid_hi_tile(FT - 1)
                    if n == 1 and not first:
                        gain_tile(i * 4 - 1)
                    if n >= 4 and n % 3 == 1:
                        gain_tile(i * 4 + (n - 4) // 3)

            down_body(0, True)
            a.activation(rms_col[:, 0, 0:1], eps_t[:, 0:1], ACT.Sqrt)
            with act.Fori(1, KT // 4) as i:
                down_body(i, False)
            take_rms(6)
            gain_tile(KT - 1)

        @block.vector
        def _(dve):
            v = nc.vector
            steps = [0]

            def link(ins):
                steps[0] += 1
                ins.then_inc(dve_steps, 1)
                dve.wait_ge(dve_steps, steps[0])

            def lo_block(b, slot, stage_slot, tiles=KB, half=None):
                half = slot % 2 if half is None else half
                dve.wait_ge(w_hi_ready, b + 1)
                v.tensor_tensor(w_lo[:, slot, 0:tiles * P],
                                stage[:, stage_slot, half * KB * P:(half * KB + tiles) * P],
                                w_hi[:, slot, 0:tiles * P].bitcast(F32), ALU.subtract).then_inc(w_lo_ready, 1)

            def lo_unit(u, s=None, mid=None):
                s = u % STAGES if s is None else s
                lo_block(u * 2, (2 * s) % RING, s)
                if mid is not None:
                    mid()
                lo_block(u * 2 + 1, (2 * s + 1) % RING, s)

            def invert(n, inv=rms_inv):
                dve.wait_ge(rms_ready, n)
                v.reciprocal(inv[:], rms[:]).then_inc(inv_ready, 1)
                dve.wait_ge(inv_ready, n)

            def mem_lo(tiles):
                for k in tiles:
                    dve.wait_ge(mem_hi_ready, k + 1)
                    v.scalar_tensor_tensor(out=alt_lo[:, k, :], in0=mem_raw[:, k, :],
                                           scalar=g_all[:, 2, k:k + 1], in1=alt_hi[:, k, :].bitcast(F32),
                                           op0=ALU.mult, op1=ALU.subtract).then_inc(mem_lo_ready, 1)

            lo_block(0, 0, 0)
            mem_lo(range(0, 8))
            lo_block(1, 1, 0)
            lo_unit(1, mid=lambda: mem_lo(range(8, 12)))
            mem_lo(range(12, 16))

            def scaled_evac(n, dst, b):
                v.tensor_reduce(dst, b[:, :].rearrange("p (e t) -> p t e", e=2), AX.X,
                                ALU.add).then_inc(halves_taken, 1)
                dve.wait_ge(halves_taken, n + 1)
                v.tensor_tensor(dst, dst, rms_inv[:], ALU.mult).then_inc(dve_evacs, 1)

            def key_evac(m):
                dve.wait_ge(blocks_used, 5 + m if m < 4 else 2 * (U_MK + m) + 2)
                scaled_evac(V_MK + m, mem_k[:, m, :], bank[m % 4])

            def softplus():
                e, z, z2, acc, w = (lam4[:, n, :] for n in (1, 2, 3, 4, 5))
                dve.wait_ge(sp_exp, 1)
                link(v.tensor_scalar(w, e, 2.0, None, ALU.add))
                link(v.reciprocal(w, w))
                link(v.tensor_tensor(z, e, w, ALU.mult))
                link(v.tensor_tensor(z2, z, z, ALU.mult))
                link(v.tensor_scalar(acc, z2, 1.0 / 15, 1.0 / 13, ALU.mult, ALU.add))
                for n in (11, 9, 7, 5, 3, 1):
                    link(v.tensor_tensor(acc, acc, z2, ALU.mult))
                    link(v.tensor_scalar(acc, acc, 1.0 / n, None, ALU.add))
                link(v.tensor_tensor(acc, acc, z, ALU.mult))
                link(v.tensor_scalar(w, par[:, 7, :], -1.0, 0.0, ALU.mult, ALU.max))
                link(v.scalar_tensor_tensor(out=w, in0=acc, scalar=2.0, in1=w, op0=ALU.mult, op1=ALU.add))
                v.tensor_scalar(lam4[:, 0, :], w, 4.0, None, ALU.mult).then_inc(lam_ready, 1)

            def normalise(k):
                dve.wait_ge(x_landed, 16)
                v.scalar_tensor_tensor(out=x_raw[:, k, :], in0=x_raw[:, k, :], scalar=g_all[:, 0, k:k + 1],
                                       in1=x_inv[:], op0=ALU.mult, op1=ALU.mult).then_inc(x_norm, 1)

            def x_lo(k):
                dve.wait_ge(act_hi_ready, k + 1)
                v.tensor_tensor(act_lo[:, k, :], x_raw[:, k, :], act_hi[:, k, :].bitcast(F32),
                                ALU.subtract).then_inc(act_lo_ready, 1)

            for u in range(2, KT):
                lo_unit(u)
                if u == 2:
                    dve.wait_ge(par_landed, 32)
                    link(v.tensor_scalar(lam4[:, 1, :], par[:, 7, :], -1.0, None, ALU.mult))
                    v.tensor_tensor(lam4[:, 0, :], par[:, 7, :], lam4[:, 1, :], ALU.max).then_inc(lam_ready, 1)
                if u == 4:
                    dve.wait_ge(rms_ready, 1)
                    v.reciprocal(rms_col[:, 1, :], rms_col[:, 0, :]).then_inc(inv_ready, 1)
                    invert(2)
                    for m in range(3):
                        key_evac(m)
                if u >= 5:
                    key_evac(u - 2)
                if u == 7:
                    softplus()
                if u == 9:
                    invert(3, x_inv)
                if u >= 11 and u < 15:
                    for k in range(4 * (u - 11), 4 * (u - 11) + 4):
                        normalise(k)
                if u >= 12:
                    for k in range(4 * (u - 12), 4 * (u - 12) + 4):
                        x_lo(k)

            def conv(c):
                dve.wait_ge(act_evacs, c + 1)
                pad = xpad[:, c % 2, :]
                link(v.tensor_scalar(xc[:, c, :], pad[:, 0:T], par[:, 0, c:c + 1], par[:, 4, c:c + 1],
                                     ALU.mult, ALU.add))
                for n in range(1, CONV):
                    ins = v.scalar_tensor_tensor(out=xc[:, c, :], in0=pad[:, n:n + T],
                                                 scalar=par[:, n, c:c + 1], in1=xc[:, c, :],
                                                 op0=ALU.mult, op1=ALU.add)
                    if n < CONV - 1:
                        link(ins)
                ins.then_inc(conv_ready, 1)

            def decay(c):
                dve.wait_ge(theta_ready, c + 1)
                link(v.tensor_scalar(den[:, c % 2, :], theta[:, c, :], 1.0, None, ALU.add))
                v.reciprocal(den[:, c % 2, :], den[:, c % 2, :]).then_inc(den_ready, 1)
                link(v.tensor_scalar(a_t[:, c % 2, :], theta[:, c, :], -1.0, 1.0, ALU.mult, ALU.add))
                dve.wait_ge(den_ready, c + 1)
                v.tensor_tensor(a_t[:, c % 2, :], a_t[:, c % 2, :], den[:, c % 2, :],
                                ALU.mult).then_inc(lru_steps, 1)

            def recur(c):
                dve.wait_ge(mult_ready, c + 1)
                dve.wait_ge(gated_in, c + 1)
                v.scalar_tensor_tensor(out=b_t[:, c % 2, :], in0=root[:, c % 4, :], scalar=2.0,
                                       in1=xc[:, c, :], op0=ALU.mult, op1=ALU.mult).then_inc(root_used, 1)
                dve.wait_ge(root_used, c + 1)
                dve.wait_ge(lru_steps, c + 1)
                v.tensor_tensor_scan(xc[:, c, :], a_t[:, c % 2, :], b_t[:, c % 2, :], 0.0,
                                     ALU.mult, ALU.add).then_inc(states_ready, 1)

            for c in range(LT):
                lo_unit(U_XB + c)
                if c < 2:
                    key_evac(KT - 2 + c)
                else:
                    conv(c - 2)
            for u in range(16):
                c = (u - 2) // 2
                if u % 2 == 0 and c >= 0:
                    decay(c)
                lo_unit(U_MV + u)
                if u < 2:
                    conv(LT - 2 + u)
                if u % 2 and c >= 0:
                    recur(c)
            decay(LT - 1)
            for u in range(4):
                lo_unit(U_K + u)
                if u == 0:
                    recur(LT - 1)

            def window_scores(k):
                g, t, L, off = k // 2, k % 2, (2, 3)[k % 2] * CHUNK, (k % 2) * CHUNK
                dve.wait_ge(scores_ready, k + 1)
                dve.wait_ge(mask_ready, 3)
                if k >= 4:
                    dve.wait_ge(turned, turns_before(k - 3))
                p = pb[:, k % 4, :, off:off + L]
                for n in range(GROUP):
                    ins = v.scalar_tensor_tensor(
                        out=pb[:, k % 4, n, off:off + L], in0=negdist[:, CHUNK - off:3 * CHUNK],
                        scalar=2.0 ** (-8.0 * (GROUP * g + n + 1) / HEADS),
                        in1=bank[4 + n % 2][:, (n // 2) * L:(n // 2) * L + L], op0=ALU.mult, op1=ALU.add)
                ins.then_inc(scores_taken, 1)
                dve.wait_ge(scores_taken, k + 1)
                mx, sink = small[:, 6 + t, :], sink_b[:, GROUP * g:GROUP * g + GROUP]
                link(v.tensor_reduce(mx, p, AX.X, ALU.max))
                link(v.tensor_tensor(mx, mx, sink, ALU.max))
                link(v.tensor_scalar(small[:, t, :], mx, -1.0, None, ALU.mult))
                v.tensor_tensor(small[:, 4 + t, :], sink, small[:, t, :], ALU.add).then_inc(max_ready, 1)

            def window_total(k):
                t = k % 2
                dve.wait_ge(probs_exp, k + 1)
                link(v.tensor_tensor(small[:, 2 + t, :], small[:, 2 + t, :], small[:, 4 + t, :], ALU.add))
                v.reciprocal(small[:, 2 + t, :], small[:, 2 + t, :]).then_inc(total_inv, 1)

            def heads_lo(k):
                g, t = k // 2, k % 2
                dve.wait_ge(y_att_hi, k + 1)
                for half in range(2):
                    rows = slice(half * HD, half * HD + HD)
                    y = (slice(LT + 2 * g, LT + 2 * g + 2), slice(t * P, t * P + P))
                    ins = v.tensor_tensor(alt_lo[rows, y[0], y[1]], head_cols(bank[6], rows, half),
                                          alt_hi[rows, y[0], y[1]].bitcast(F32), ALU.subtract)
                ins.then_inc(y_att_lo, 1)

            def window(j):
                if 0 <= j - 6 < GK:
                    window_total(j - 6)
                if 0 <= j - 4 < GK:
                    window_scores(j - 4)

            def gate_states(c):
                dve.wait_ge(act_evacs, A_GT + c + 1)
                v.tensor_tensor(xc[:, c, :], xc[:, c, :], lru_g[:, c % 2, :], ALU.mult).then_inc(y_lru_f, 1)

            def y_lo(c):
                dve.wait_ge(y_lru_hi, c + 1)
                v.tensor_tensor(alt_lo[:, c, :], xc[:, c, :], alt_hi[:, c, :].bitcast(F32),
                                ALU.subtract).then_inc(y_lru_lo, 1)

            def mid(j):
                if 0 <= j - 9 < GK:
                    heads_lo(j - 9)
                if j >= 12 and j % 2 == 0:
                    gate_states(j - 12)
                    gate_states(j - 11)
                    y_lo(j - 12)
                    y_lo(j - 11)

            for j in range(16):
                lo_unit(U_Q + j, mid=lambda: mid(j))
                window(j)

            def h_evac(m, b, evacs, gain, phase):
                v.tensor_tensor(h[:, m, :], h[:, m, :], b[:, T:2 * T], ALU.add).then_inc(halves_taken, 1)
                dve.wait_ge(halves_taken, m + (evacs + 1))
                v.tensor_tensor(h[:, m, :], h[:, m, :], b[:, 0:T], ALU.add).then_inc(dve_evacs, 1)
                if gain is not None:
                    dve.wait_ge(act_hi_ready, m + (KT * (phase + 1) + 1))
                    v.scalar_tensor_tensor(out=act_lo[:, m, :], in0=h[:, m, :],
                                           scalar=g_all[:, gain, bass.ds(m, 1)],
                                           in1=act_hi[:, m, :].bitcast(F32), op0=ALU.mult,
                                           op1=ALU.subtract).then_inc(act_lo_ready, 1)

            def out_tile(m, s):
                dve.wait_ge(blocks_used, m * 2 + (2 * U_OUT + 2))
                h_evac(m, bank[s % 4], V_OUT, 1, 0)

            def mo_tile(m, s):
                dve.wait_ge(blocks_used, m * 2 + (2 * U_MO + 2))
                h_evac(m, bank[s % 4], V_MO, 3, 1)

            lo_unit(U_OUT, mid=lambda: mid(16))
            gate_states(6)
            y_lo(6)

            def last_gate():
                gate_states(7)
                y_lo(7)

            lo_unit(U_OUT + 1, mid=last_gate)
            dve.wait_ge(res_landed, 16)
            for s in range(2, 4):
                lo_unit(U_OUT + s)
                out_tile(s - 2, s - 2)
            with dve.Fori(1, KT // 4) as i:
                for s in range(4):
                    lo_unit(i * 4 + (U_OUT + s), s)
                    out_tile(i * 4 + (s - 2), s + 2)

            def query_evac(j):
                dve.wait_ge(blocks_used, 2 * (U_MQ + j) + 2)
                if j >= 2 * MHT:
                    dve.wait_ge(m_scores, j // MHT - 1)
                scaled_evac(V_MQ + j, mq[:, j // MHT % 2, j % MHT, :], bank[j % 4])

            def m_maximum(hd):
                dve.wait_ge(m_scores, hd + 1)
                link(v.tensor_reduce(msmall[:, 0, :], bank[4][:, :].rearrange("p (a m) -> p a m", a=2),
                                     AX.X, ALU.max))
                v.tensor_scalar(msmall[:, 1, :], msmall[:, 0, :], -(D // MH) ** -0.5, None,
                                ALU.mult).then_inc(m_max, 1)

            def m_divide(hd):
                dve.wait_ge(m_exp, 2 * hd + 2)
                link(v.reciprocal(msmall[:, 3, :], msmall[:, 2, :]))
                for tt in range(2):
                    ins = v.tensor_scalar(mp[:, tt, :], mp[:, tt, :], msmall[:, 3, tt:tt + 1], None, ALU.mult)
                ins.then_inc(m_probs, 1)

            def m_out(hd):
                for half in range(2):
                    dve.wait_ge(m_heads, 2 * hd + half + 1)
                    src = bank[6 + half][:, :].rearrange("p (m t) -> p m t", m=MHT // 2)
                    first = MHT * hd + MHT // 2 * half
                    tiles = slice(first, first + MHT // 2)
                    link(v.tensor_copy(alt_hi[:, tiles, :], src))
                    v.tensor_tensor(alt_lo[:, tiles, :], src, alt_hi[:, tiles, :].bitcast(F32),
                                    ALU.subtract).then_inc(o_lo_ready, 1)

            for j in range(16):
                divide = (lambda hd=(j - 7) // 4: m_divide(hd)) if j >= 7 and j % 4 == 3 else None
                lo_unit(U_MQ + j, mid=divide)
                if j < 2:
                    out_tile(14 + j, 2 + j)
                if j == 2:
                    invert(4)
                if j >= 2:
                    query_evac(j - 2)
                if j in (6, 10, 14):
                    m_maximum((j - 6) // 4)
                if j in (9, 13):
                    m_out((j - 9) // 4)
            lo_unit(U_MO)
            query_evac(14)
            lo_unit(U_MO + 1)
            query_evac(15)
            m_out(2)
            m_maximum(3)
            m_divide(3)
            for s in range(2, 4):
                lo_unit(U_MO + s, mid=(lambda: m_out(3)) if s == 2 else None)
                mo_tile(s - 2, s - 2)
            with dve.Fori(1, KT // 4) as i:
                for s in range(4):
                    lo_unit(i * 4 + (U_MO + s), s)
                    mo_tile(i * 4 + (s - 2), s + 2)

            def gate_evac(p, b):
                dve.wait_ge(blocks_used, p * 4 + (2 * U_GU + 2))
                scaled_evac(p * 2 + V_GU, gate_s[:], b)

            def up_evac(p, b):
                dve.wait_ge(blocks_used, p * 4 + (2 * U_GU + 4))
                scaled_evac(p * 2 + (V_GU + 1), up_s[:], b)
                dve.wait_ge(dve_evacs, p * 2 + (V_GU + 2))
                dve.wait_ge(silu_ready, p + 1)
                v.tensor_tensor(up_s[:], up_s[:], gate_s[:], ALU.mult).then_inc(hid_ready, 1)
                dve.wait_ge(hid_hi_ready, p + 1)
                v.tensor_tensor(hid_lo[:, p, :], up_s[:], hid_hi[:, p, :].bitcast(F32),
                                ALU.subtract).then_inc(hid_lo_ready, 1)

            lo_unit(U_GU)
            mo_tile(14, 2)
            lo_unit(U_GU + 1)
            mo_tile(15, 3)
            lo_unit(U_GU + 2)
            invert(5)
            gate_evac(0, bank[0])
            lo_unit(U_GU + 3)
            up_evac(0, bank[1])
            with dve.Fori(1, FT // 2) as i:
                for s in range(4):
                    lo_unit(i * 4 + (U_GU + s), s)
                    (up_evac if s % 2 else gate_evac)(i * 2 + (s // 2 - 1), bank[(s + 2) % 4])

            def down_tile(m, b):
                dve.wait_ge(blocks_used, m * 6 + (2 * U_DN + 6))
                h_evac(m, b, V_DN, None, 2)

            def down_body(i, first):
                for n in range(12):
                    u = i * 12 + (U_DN + n)
                    for half in range(2):
                        lo_block(u * 2 + half, (2 * n + half) % RING, n % STAGES,
                                 4 if n % 3 == 2 and half else KB, half)
                    if first and n == 0:
                        gate_evac(FT - 1, bank[2])
                    if first and n == 1:
                        up_evac(FT - 1, bank[3])
                    if not first and n == 1:
                        down_tile(i * 4 - 1, bank[3])
                    if n >= 4 and n % 3 == 1:
                        down_tile(i * 4 + (n - 4) // 3, bank[(n - 4) // 3])

            down_body(0, True)
            with dve.Fori(1, KT // 4) as i:
                down_body(i, False)
            down_tile(KT - 1, bank[3])
            dve.wait_ge(dve_evacs, V_DN + KT)
            v.tensor_tensor(up_s[:], h[:, KT - 1, :], h[:, KT - 1, :], ALU.mult).then_inc(last_squared, 1)
            invert(6)
            dve.wait_ge(gained, KT)
            for first, tiles in DVE_OUT:
                o = h[:, first:first + tiles, :]
                v.tensor_tensor(o, o, rms_inv[:].unsqueeze(1).broadcast_to([P, tiles, T]),
                                ALU.mult).then_inc(outs_dve, 1)

        @block.tensor
        def _(pe):
            t = nc.tensor

            def product(out, pair, slot, kt_w, kt, first, last):
                wh = w_hi[:, slot, kt_w * P:kt_w * P + P]
                wl = w_lo[:, slot, kt_w * P:kt_w * P + P]
                if out.shape[1] == 2 * T:
                    if last:
                        t.matmul(out[:, 0:T], wl, pair[:, 0, kt, :], start=False, stop=False)
                        return t.matmul(out, wh, pair[:, :, kt, :], start=False, stop=True)
                    t.matmul(out, wh, pair[:, :, kt, :], start=first, stop=False)
                    return t.matmul(out[:, 0:T], wl, pair[:, 0, kt, :], start=False, stop=False)
                t.matmul(out, wh, pair[:, 0, kt, :], start=first, stop=False)
                t.matmul(out, wh, pair[:, 1, kt, :], start=False, stop=False)
                return t.matmul(out, wl, pair[:, 0, kt, :], start=False, stop=last)

            def half_unit(b, slot, out, pair, kts, last_kt, waits=(), w_from=0, inc=1):
                pe.wait_ge(w_lo_ready, b + 1)
                for n, kt in enumerate(kts):
                    for at_kt, counter, value in waits:
                        if at_kt == kt:
                            pe.wait_ge(counter, value)
                    ins = product(out, pair, slot, w_from + n, kt, kt == 0, kt == last_kt)
                if inc:
                    ins.then_inc(blocks_used, inc)

            def unit(u, out, pair, s=None, waits=(), mid=None):
                s = u % STAGES if s is None else s
                half_unit(u * 2, (2 * s) % RING, out, pair, range(0, KB), KT - 1, waits)
                if mid is not None:
                    mid()
                half_unit(u * 2 + 1, (2 * s + 1) % RING, out, pair, range(KB, KT), KT - 1, waits)

            def sums():
                t.matmul(bank[7][:, 0:T], ones[:, :], sq_sum[:, :], start=True, stop=True).then_inc(sums_ready, 1)

            pe.wait_ge(consts_ready, 3)
            for half in range(2):
                kts = range(half * KB, half * KB + KB)
                for n in range(4):
                    waits = [(k, mem_lo_ready, k + 1) for k in kts] if n == 0 else ()
                    half_unit(4 * half + n, n, bank[n][:, :], alts, kts, KT - 1, waits)
                    if half == 1 and n == 2:
                        pe.wait_ge(sq_ready, 1)
                        sums()
                        for tt in range(2):
                            ins = t.matmul(bank[7][:, T + tt:T + tt + 1], sq_sum[:, tt * P:tt * P + P],
                                           ones[:, 0:1], start=True, stop=True)
                        ins.then_inc(sums_ready, 1)
            for u in range(4, KT // 2):
                pe.wait_ge(dve_evacs, u - 3)
                unit(U_MK + u, bank[u % 4][:, :], alts)
            pe.wait_ge(sq_ready, 2)
            pe.wait_ge(rms_ready, 2)
            sums()
            with pe.Fori(2, KT // 4) as i:
                for s in range(4):
                    pe.wait_ge(dve_evacs, i * 4 + (s - 3))
                    unit(i * 4 + (U_MK + s), bank[s][:, :], alts, s)

            def gates(c):
                pe.wait_ge(conv_ready, c + 1)
                if c == 0:
                    pe.wait_ge(wg_landed, 64)
                if c >= 2:
                    pe.wait_ge(sig_ready, 2 * c - 2)
                for n in range(2):
                    ins = t.matmul(bank[4 + c % 2][:, n * T:n * T + T], wg[:, n, c, :], xc[:, c, :],
                                   start=True, stop=True)
                ins.then_inc(gates_ready, 1)

            for c in range(LT):
                if c < 4:
                    pe.wait_ge(dve_evacs, KT - 3 + c)
                else:
                    pe.wait_ge(act_evacs, c - 3)
                waits = [(0, act_lo_ready, KT)] if c == 0 else ()
                unit(U_XB + c, bank[c % 4][:, 0:T], acts, waits=waits)
                if c >= 2:
                    gates(c - 2)

            def value_block(b, slot, outs, width, hi, lo, kts):
                pe.wait_ge(w_lo_ready, b + 1)
                for m, kt in enumerate(kts):
                    wh = w_hi[:, slot, m * width:m * width + width]
                    wl = w_lo[:, slot, m * width:m * width + width]
                    for tt in range(2):
                        xh, xl = hi[:, kt, tt * P:tt * P + P], lo[:, kt, tt * P:tt * P + P]
                        t.matmul(outs[tt], xh, wh, start=kt == 0, stop=False)
                        t.matmul(outs[tt], xh, wl, start=False, stop=False)
                        ins = t.matmul(outs[tt], xl, wh, start=False, stop=kt == KT - 1)
                ins.then_inc(blocks_used, 1)

            for u in range(16):
                n = u // 4
                if u % 4 == 0:
                    pe.wait_ge(act_evacs, A_MV - 2 + 2 * n)
                for half in range(2):
                    b = 2 * (U_MV + u) + half
                    kt0 = 4 * (u % 4) + 2 * half
                    value_block(b, b % RING, [bank[2 * (n % 2) + tt][:, :] for tt in range(2)], 512,
                                alt_hi, alt_lo, range(kt0, kt0 + 2))
                if u < 2:
                    gates(LT - 2 + u)
            for m in range(2):
                pe.wait_ge(act_evacs, A_MV + 6)
                unit(U_K + m, bank[m][:, 0:T], acts)
            pe.wait_ge(act_evacs, A_K)
            for u in range(2):
                for half in range(2):
                    b = 2 * (U_V + u) + half
                    kt0 = 8 * u + 4 * half
                    value_block(b, b % RING, [bank[2 + tt][:, 0:T] for tt in range(2)], T,
                                act_hi, act_lo, range(kt0, kt0 + 4))

            def scores(k):
                g, tt, L, off = k // 2, k % 2, (2, 3)[k % 2] * CHUNK, (k % 2) * CHUNK
                pe.wait_ge(act_evacs, A_Q + 2 * g + 2)
                if k >= 1:
                    pe.wait_ge(scores_taken, k)
                for n in range(GROUP):
                    rows = slice((n % 2) * HD, (n % 2) * HD + HD)
                    ins = t.matmul(bank[4 + n % 2][:, (n // 2) * L:(n // 2) * L + L],
                                   qs[rows, 2 * g + n // 2, tt * P:tt * P + P],
                                   kd[rows, g, off:off + L], start=True, stop=True)
                ins.then_inc(scores_ready, 1)

            def turn(k):
                pe.wait_ge(probs_ready, k + 1)
                if k >= 1:
                    pe.wait_ge(y_att_lo, k)
                for kb in range(1 + k % 2):
                    for n in range(GROUP):
                        ins = t.transpose(bank[6 + kb][:, n * P:n * P + P],
                                          pb[:, k % 4, n, kb * P:kb * P + P], ident[:, :])
                    ins.then_inc(turned, 1)

            def heads(k):
                g = k // 2
                pe.wait_ge(pt_ready, turns_before(k + 1))
                for kb in range(1 + k % 2):
                    ins = t.matmul(bank[6][:, :], vd[:, kb, g, :, :].rearrange("p e d -> p (e d)"),
                                   pt[:, kb, :], start=kb == 0, stop=kb == k % 2)
                ins.then_inc(heads_ready, 1)

            for j in range(16):
                pe.wait_ge(act_evacs, A_K + 1 + j)
                mid = (lambda k=j - 7: heads(k)) if 0 <= j - 7 < GK else None
                unit(U_Q + j, bank[j % 4][:, 0:T], acts, mid=mid)
                if 0 <= j - 2 < GK:
                    scores(j - 2)
                if 0 <= j - 6 < GK:
                    turn(j - 6)

            y_waits = [(0, y_lru_lo, 7), (7, y_lru_lo, 8), (8, y_att_lo, 6), (14, y_att_lo, 8)]
            with pe.Fori(0, KT // 4) as i:
                for s in range(4):
                    pe.wait_ge(act_evacs, A_GT + 5 + s)
                    pe.wait_ge(dve_evacs, i * 4 + (V_OUT + s - 3))
                    unit(i * 4 + (U_OUT + s), bank[s][:, :], alts, s, waits=y_waits)

            def m_scores_of(hd):
                pe.wait_ge(dve_evacs, V_MQ + MHT * hd + MHT)
                if hd >= 1:
                    pe.wait_ge(m_exp, 2 * hd)
                for tt in range(2):
                    for k in range(MHT):
                        ins = t.matmul(bank[4][:, tt * T:tt * T + T], mq[:, hd % 2, k, tt * P:tt * P + P],
                                       mem_k[:, MHT * hd + k, :], start=k == 0, stop=k == MHT - 1)
                ins.then_inc(m_scores, 1)

            def m_turn(hd):
                pe.wait_ge(m_probs, hd + 1)
                if hd >= 1:
                    pe.wait_ge(m_pt, hd)
                for a in range(2):
                    for tt in range(2):
                        ins = t.transpose(bank[5][:, a * T + tt * P:a * T + tt * P + P],
                                          mp[:, tt, a * P:a * P + P], ident[:, :])
                ins.then_inc(m_turned, 1)

            def m_heads_of(hd):
                pe.wait_ge(m_pt, hd + 1)
                if hd >= 1:
                    pe.wait_ge(o_lo_ready, 2 * hd)
                for m in range(MHT):
                    for a in range(2):
                        c = (MHT * hd + m) * P
                        ins = t.matmul(o_bank[:, m * T:m * T + T], mem_v[:, a, c:c + P], mpt[:, a, :],
                                       start=a == 0, stop=a == 1)
                    if m % 2:
                        ins.then_inc(m_heads, 1)

            for j in range(16):
                pe.wait_ge(dve_evacs, V_MQ - 3 + j)
                waits = [(0, act_lo_ready, 2 * KT - 2), (14, act_lo_ready, 2 * KT - 1),
                         (15, act_lo_ready, 2 * KT)] if j == 0 else ()
                unit(U_MQ + j, bank[j % 4][:, :], acts, waits=waits)
                if j == 0:
                    pe.wait_ge(summed, KT)
                    sums()
                if j in (4, 8, 12):
                    m_scores_of(j // 4 - 1)
                if j in (6, 10, 14):
                    m_turn((j - 6) // 4)
                if j in (7, 11, 15):
                    m_heads_of((j - 7) // 4)

            def mo_part(u, half, kts, inc, w_from=0):
                b = 2 * (U_MO + u) + half
                half_unit(b, b % RING, bank[u][:, :], alts, kts, KT - 1,
                          waits=[(0, o_lo_ready, 4), (8, o_lo_ready, 6), (12, o_lo_ready, 7),
                                 (14, o_lo_ready, 8)],
                          w_from=w_from, inc=inc)

            for u in range(2):
                pe.wait_ge(dve_evacs, V_MO - 3 + u)
            mo_part(0, 0, range(0, 8), 1)
            m_scores_of(3)
            mo_part(1, 0, range(0, 8), 0)
            mo_part(0, 1, range(8, 12), 0)
            m_turn(3)
            mo_part(1, 1, range(8, 12), 0)
            m_heads_of(3)
            mo_part(0, 1, range(12, 14), 0, 4)
            mo_part(1, 1, range(12, 14), 0, 4)
            mo_part(0, 1, range(14, 16), 2, 6)
            mo_part(1, 1, range(14, 16), 1, 6)
            for s in range(2, 4):
                pe.wait_ge(dve_evacs, V_MO - 3 + s)
                unit(U_MO + s, bank[s][:, :], alts)
            with pe.Fori(1, KT // 4) as i:
                for s in range(4):
                    pe.wait_ge(dve_evacs, i * 4 + (V_MO + s - 3))
                    unit(i * 4 + (U_MO + s), bank[s][:, :], alts, s)

            def gu_body(i, first):
                for s in range(4):
                    pe.wait_ge(dve_evacs, i * 4 + (V_GU + s - 3))
                    waits = [(0, act_lo_ready, 3 * KT - 2), (14, act_lo_ready, 3 * KT - 1),
                             (15, act_lo_ready, 3 * KT)] if first and s == 0 else ()
                    unit(i * 4 + (U_GU + s), bank[s][:, :], acts, s, waits=waits)
                    if first and s == 0:
                        pe.wait_ge(summed, 2 * KT)
                        sums()

            gu_body(0, True)
            with pe.Fori(1, FT // 2) as i:
                gu_body(i, False)

            with pe.Fori(0, KT // 4) as i:
                for n in range(12):
                    m = n // 3
                    if n % 3 == 0:
                        pe.wait_ge(dve_evacs, i * 4 + (V_DN + m - 3))
                    u = i * 12 + (U_DN + n)
                    kt0, tiles = DN_PARTS[n % 3]
                    for half in range(2):
                        kts = range(kt0 + KB * half, kt0 + min(KB * half + KB, tiles))
                        half_unit(u * 2 + half, (2 * n + half) % RING, bank[m][:, :], hids,
                                  kts, FT - 1, waits=[(0, hid_lo_ready, FT - 2), (FT - 2, hid_lo_ready, FT - 1),
                                                      (FT - 1, hid_lo_ready, FT)])
            pe.wait_ge(summed, 3 * KT - 1)
            t.matmul(bank[7][:, 0:T], ones[:, :], sq_sum[:, :], start=True, stop=False)
            pe.wait_ge(last_squared, 1)
            t.matmul(bank[7][:, 0:T], ones[:, :], up_s[:, :], start=False, stop=True).then_inc(sums_ready, 1)


def kernel(**inputs):
    import numpy as np
    from concourse import bacc
    from concourse.bass_utils import run_bass_kernel_spmd

    a = {k: np.asarray(v) for k, v in inputs.items()}

    def tall(x):
        return x.T.reshape(-1, P, x.shape[0]).transpose(1, 0, 2)

    def tiles(w):
        r, c = w.shape
        return w.reshape(r // P, P, c // P, P).transpose(2, 1, 0, 3).reshape(c // P, P, r)

    def slices(w, width):
        r, c = w.shape
        per = UNIT // width
        return (w.reshape(r // (per * P), per, P, c // width, width).transpose(3, 0, 2, 1, 4)
                .reshape(-1, P, UNIT))

    def column(x):
        return x.reshape(-1, P).T

    w_in, w_mkv, w_gu = a["w_in"][0], a["w_mkv"][0], a["w_gate_up"][0]
    o_q = 2 * LRU
    o_k = o_q + HEADS * HD
    o_v = o_k + KV_HEADS * HD
    w_mk = tiles(w_mkv[:, :D])
    w_mk = np.concatenate([w_mk[:4].reshape(4, P, 2, KB * P).transpose(2, 0, 1, 3).reshape(4, 2, P, KB * P)
                           .transpose(0, 2, 1, 3).reshape(4, P, UNIT), w_mk[4:]])
    gate_up = np.stack([tiles(w_gu[:, :D_FF]), tiles(w_gu[:, D_FF:])], 1).reshape(-1, P, UNIT)
    w_units = np.concatenate([
        w_mk, tiles(w_in[:, :LRU]), slices(w_mkv[:, D:], 512),
        tiles(w_in[:, o_k:o_v]), slices(w_in[:, o_v:], T), tiles(w_in[:, o_q:o_k]),
        tiles(w_in[:, LRU:o_q]), tiles(a["w_out"][0]), tiles(a["w_mq"][0]), tiles(a["w_mo"][0]), gate_up])
    blocks = np.stack([a["w_rgate"][0], a["w_igate"][0]])
    arrays = {
        "xT": tall(a["x"][0]),
        "memT": tall(a["mem"][0]),
        "w_units": w_units,
        "w_down": tiles(a["w_down"][0]),
        "gains": np.stack([column(a[n]) for n in ("norm_mix", "norm_mem_q", "norm_mem_kv", "norm_ffn",
                                                   "norm_final")], 1),
        "lru_par": np.stack([*(column(a["conv_w"][0, j]) for j in range(CONV)),
                             *(column(a[n]) for n in ("conv_b", "b_rgate", "b_igate", "lru_lambda"))], 1),
        "w_gates": blocks.reshape(2, LT, 2, HD, HD).transpose(0, 2, 3, 1, 4),
        "sinks": a["attn_sinks"].reshape(-1),
    }
    nc = bacc.Bacc("TRN2", target_bir_lowering=False, num_devices=1)
    arrays = {k: np.ascontiguousarray(v) for k, v in arrays.items()}
    args = [nc.dram_tensor(k, v.shape, mybir.dt.from_np(v.dtype), kind="ExternalInput").ap()
            for k, v in arrays.items()]
    out = nc.dram_tensor("outT", (P, KT, T), F32, kind="ExternalOutput").ap()
    hybrid_block(nc, *args, out)
    r = run_bass_kernel_spmd(nc, [arrays], core_ids=[0])
    got = r.results[0]["outT"]
    return got.transpose(2, 1, 0).reshape(1, T, D)
```
